# Optimizing a Trainium2 kernel written in Bass

```python
import math
import jax, jax.numpy as jnp
from jax import lax
import numpy as np

D_MODEL = 2048
BATCH = 1
SEQ = 512
DEPTH = 2

D_MIX = D_MODEL
MLA_HEADS = 6
QK_NOPE = 128
QK_ROPE = 64
QK_HEAD = QK_NOPE + QK_ROPE
V_HEAD = 128
Q_LORA = 512
KV_LORA = 256
MLA_WIDTH = MLA_HEADS * V_HEAD
ROPE_THETA = 10000.0
Q_BLOCK = 128
CONV_WIDTH = 512
CONV_K = 31
SSD_HEADS = 12
SSD_HEAD_DIM = 64
SSD_WIDTH = SSD_HEADS * SSD_HEAD_DIM
SSD_GROUPS = 2
SSD_STATE = 128
SSD_CONV_K = 4
SSD_CHUNK = 128
SSD_XBC = SSD_WIDTH + 2 * SSD_GROUPS * SSD_STATE

NORM_EPS = 1e-6
LN_EPS = 1e-5

IN_SPLITS = (Q_LORA, KV_LORA, QK_ROPE, MLA_WIDTH,
             2 * CONV_WIDTH, CONV_WIDTH,
             SSD_WIDTH, SSD_XBC, SSD_HEADS)
D_IN_PROJ = sum(IN_SPLITS)

kernel_name = 'hybrid_mla_conformer_ssd_parallel'

def rms_norm(x, g, eps=NORM_EPS):
    xf = x.astype(jnp.float32)
    y = xf * lax.rsqrt(jnp.mean(xf * xf, axis=-1, keepdims=True) + eps)
    return (y * g.astype(jnp.float32)).astype(x.dtype)

def layer_norm(x, g, b, eps=LN_EPS):
    xf = x.astype(jnp.float32)
    mu = jnp.mean(xf, axis=-1, keepdims=True)
    var = jnp.mean(jnp.square(xf - mu), axis=-1, keepdims=True)
    y = (xf - mu) * lax.rsqrt(var + eps)
    return (y * g.astype(jnp.float32) + b.astype(jnp.float32)).astype(x.dtype)

def causal_depthwise_conv(x, w, b):
    k = w.shape[0]
    y = lax.conv_general_dilated(
        x, w[:, None, :].astype(x.dtype), window_strides=(1,), padding=[(k - 1, 0)],
        dimension_numbers=('NWC', 'WIO', 'NWC'), feature_group_count=x.shape[-1])
    return y + b.astype(x.dtype)

def apply_rope(x, pos):
    half = x.shape[-1] // 2
    inv_freq = ROPE_THETA ** (-jnp.arange(half, dtype=jnp.float32) / half)
    ang = pos.astype(jnp.float32)[:, None] * inv_freq[None, :]
    cos = jnp.cos(ang)[None, :, None, :]
    sin = jnp.sin(ang)[None, :, None, :]
    xf = x.astype(jnp.float32)
    x1, x2 = xf[..., :half], xf[..., half:]
    return jnp.concatenate([x1 * cos - x2 * sin, x2 * cos + x1 * sin], axis=-1).astype(x.dtype)

def blocked_causal_attention(q, k, v):
    bsz, s, h, dqk = q.shape
    dv = v.shape[-1]
    nb = s // Q_BLOCK
    scale = 1.0 / math.sqrt(dqk)
    qb = q.reshape(bsz, nb, Q_BLOCK, h, dqk).transpose(1, 0, 2, 3, 4)
    kpos = jnp.arange(s)

    def one_block(args):
        qi, i = args
        sc = jnp.einsum('bqhd,bkhd->bhqk', qi, k, preferred_element_type=jnp.float32) * scale
        qpos = i * Q_BLOCK + jnp.arange(Q_BLOCK)
        mask = kpos[None, :] <= qpos[:, None]
        sc = jnp.where(mask[None, None], sc, -jnp.inf)
        p = jax.nn.softmax(sc, axis=-1).astype(v.dtype)
        return jnp.einsum('bhqk,bkhd->bqhd', p, v)

    o = lax.map(one_block, (qb, jnp.arange(nb)))
    return o.transpose(1, 0, 2, 3, 4).reshape(bsz, s, h * dv)

def mla_mixer(c_q, c_kv, k_pe, q_a_norm, w_q_b, kv_a_norm, w_kv_b, q_norm, k_norm):
    bsz, s, _ = c_q.shape
    q = (rms_norm(c_q, q_a_norm) @ w_q_b).reshape(bsz, s, MLA_HEADS, QK_HEAD)
    kv = (rms_norm(c_kv, kv_a_norm) @ w_kv_b).reshape(bsz, s, MLA_HEADS, QK_NOPE + V_HEAD)
    k_nope, v = kv[..., :QK_NOPE], kv[..., QK_NOPE:]
    k_pe_h = jnp.broadcast_to(k_pe[:, :, None, :], (bsz, s, MLA_HEADS, QK_ROPE))
    k = jnp.concatenate([k_nope, k_pe_h], axis=-1)
    q = rms_norm(q, q_norm)
    k = rms_norm(k, k_norm)
    pos = jnp.arange(s)
    q = jnp.concatenate([q[..., :QK_NOPE], apply_rope(q[..., QK_NOPE:], pos)], axis=-1)
    k = jnp.concatenate([k[..., :QK_NOPE], apply_rope(k[..., QK_NOPE:], pos)], axis=-1)
    return blocked_causal_attention(q, k, v)

def conformer_conv_mixer(u, w_dw, b_dw, ln_g, ln_b, w_pw):
    a, g = u[..., :CONV_WIDTH], u[..., CONV_WIDTH:]
    h = a * jax.nn.sigmoid(g)
    h = causal_depthwise_conv(h, w_dw, b_dw)
    h = jax.nn.silu(layer_norm(h, ln_g, ln_b))
    return h @ w_pw

def ssd_chunked(x, dt, a_neg, bm, cm):
    bsz, s, h, p = x.shape
    g, n = bm.shape[2], bm.shape[3]
    r = h // g
    l = SSD_CHUNK
    c = s // l
    xf = x.astype(jnp.float32).reshape(bsz, c, l, g, r, p)
    dtc = dt.reshape(bsz, c, l, g, r)
    bc = bm.astype(jnp.float32).reshape(bsz, c, l, g, n)
    cc = cm.astype(jnp.float32).reshape(bsz, c, l, g, n)
    xdt = xf * dtc[..., None]
    a_cs = jnp.cumsum(dtc * a_neg.reshape(g, r), axis=2)
    seg = a_cs[:, :, :, None] - a_cs[:, :, None, :]
    causal = jnp.tril(jnp.ones((l, l), dtype=bool))
    decay = jnp.exp(jnp.where(causal[None, None, :, :, None, None], seg, -jnp.inf))
    cb = jnp.einsum('bclgn,bcsgn->bclsg', cc, bc)
    y_diag = jnp.einsum('bclsg,bclsgr,bcsgrp->bclgrp', cb, decay, xdt)
    decay_to_end = jnp.exp(a_cs[:, :, -1:] - a_cs)
    states = jnp.einsum('bclgn,bclgr,bclgrp->bcgrpn', bc, decay_to_end, xdt)
    chunk_decay = jnp.exp(a_cs[:, :, -1])

    def step(hstate, inp):
        st, dec = inp
        return hstate * dec[..., None, None] + st, hstate

    h0 = jnp.zeros((bsz, g, r, p, n), jnp.float32)
    _, prev = lax.scan(step, h0, (states.transpose(1, 0, 2, 3, 4, 5), chunk_decay.transpose(1, 0, 2, 3)))
    prev = prev.transpose(1, 0, 2, 3, 4, 5)
    y_off = jnp.einsum('bclgn,bcgrpn,bclgr->bclgrp', cc, prev, jnp.exp(a_cs))
    return (y_diag + y_off).reshape(bsz, s, h, p)

def ssd_mixer(z, xbc, dt_raw, conv_w, conv_b, dt_bias, a_log, d_skip, norm_g):
    bsz, s, _ = z.shape
    xbc = jax.nn.silu(causal_depthwise_conv(xbc, conv_w, conv_b))
    xs = xbc[..., :SSD_WIDTH].reshape(bsz, s, SSD_HEADS, SSD_HEAD_DIM)
    bm = xbc[..., SSD_WIDTH:SSD_WIDTH + SSD_GROUPS * SSD_STATE].reshape(bsz, s, SSD_GROUPS, SSD_STATE)
    cm = xbc[..., SSD_WIDTH + SSD_GROUPS * SSD_STATE:].reshape(bsz, s, SSD_GROUPS, SSD_STATE)
    dt = jax.nn.softplus(dt_raw.astype(jnp.float32) + dt_bias.astype(jnp.float32))
    a_neg = -jnp.exp(a_log.astype(jnp.float32))
    y = ssd_chunked(xs, dt, a_neg, bm, cm)
    y = y + d_skip.astype(jnp.float32)[:, None] * xs.astype(jnp.float32)
    y = y.reshape(bsz, s, SSD_WIDTH).astype(z.dtype)
    return rms_norm(y * jax.nn.silu(z), norm_g)

def hybrid_layer(x, norm_g, w_in, q_a_norm, w_q_b, kv_a_norm, w_kv_b, q_norm, k_norm,
                 conv_dw_w, conv_dw_b, conv_ln_g, conv_ln_b, conv_pw_w,
                 ssd_conv_w, ssd_conv_b, ssd_dt_bias, ssd_A_log, ssd_D, ssd_norm_g, w_out):
    h = rms_norm(x, norm_g)
    u = h @ w_in
    offs = np.cumsum(IN_SPLITS)[:-1].tolist()
    c_q, c_kv, k_pe, g_mla, u_conv, g_conv, z, xbc, dt_raw = jnp.split(u, offs, axis=-1)
    o_mla = mla_mixer(c_q, c_kv, k_pe, q_a_norm, w_q_b, kv_a_norm, w_kv_b, q_norm, k_norm) * jax.nn.silu(g_mla)
    o_conv = conformer_conv_mixer(u_conv, conv_dw_w, conv_dw_b, conv_ln_g, conv_ln_b, conv_pw_w) * jax.nn.silu(g_conv)
    o_ssd = ssd_mixer(z, xbc, dt_raw, ssd_conv_w, ssd_conv_b, ssd_dt_bias, ssd_A_log, ssd_D, ssd_norm_g)
    y = jnp.concatenate([o_mla, o_conv, o_ssd], axis=-1) @ w_out
    return x + y

def setup_inputs(seed: int = 0) -> dict:
    key = jax.random.key(seed)
    ks = jax.random.split(key, 24)
    f32 = jnp.float32

    def nrm(k, shape, fan_in):
        return jax.random.normal(k, shape, f32) * (fan_in ** -0.5)

    def gain(k, shape):
        return 1.0 + 0.02 * jax.random.normal(k, shape, f32)

    def small(k, shape):
        return 0.02 * jax.random.normal(k, shape, f32)

    dt0 = jnp.exp(jax.random.uniform(ks[17], (DEPTH, SSD_HEADS), f32, math.log(1e-3), math.log(1e-1)))
    return {
        'x': jax.random.normal(ks[0], (BATCH, SEQ, D_MODEL), f32),
        'norm_g': gain(ks[1], (DEPTH, D_MODEL)),
        'w_in': nrm(ks[2], (DEPTH, D_MODEL, D_IN_PROJ), D_MODEL),
        'q_a_norm': gain(ks[3], (DEPTH, Q_LORA)),
        'w_q_b': nrm(ks[4], (DEPTH, Q_LORA, MLA_HEADS * QK_HEAD), Q_LORA),
        'kv_a_norm': gain(ks[5], (DEPTH, KV_LORA)),
        'w_kv_b': nrm(ks[6], (DEPTH, KV_LORA, MLA_HEADS * (QK_NOPE + V_HEAD)), KV_LORA),
        'q_norm': gain(ks[7], (DEPTH, QK_HEAD)),
        'k_norm': gain(ks[8], (DEPTH, QK_HEAD)),
        'conv_dw_w': nrm(ks[9], (DEPTH, CONV_K, CONV_WIDTH), CONV_K),
        'conv_dw_b': small(ks[10], (DEPTH, CONV_WIDTH)),
        'conv_ln_g': gain(ks[11], (DEPTH, CONV_WIDTH)),
        'conv_ln_b': small(ks[12], (DEPTH, CONV_WIDTH)),
        'conv_pw_w': nrm(ks[13], (DEPTH, CONV_WIDTH, CONV_WIDTH), CONV_WIDTH),
        'ssd_conv_w': nrm(ks[14], (DEPTH, SSD_CONV_K, SSD_XBC), SSD_CONV_K),
        'ssd_conv_b': small(ks[15], (DEPTH, SSD_XBC)),
        'ssd_dt_bias': dt0 + jnp.log(-jnp.expm1(-dt0)),
        'ssd_A_log': jnp.log(jax.random.uniform(ks[18], (DEPTH, SSD_HEADS), f32, 1.0, 16.0)),
        'ssd_D': gain(ks[19], (DEPTH, SSD_HEADS)),
        'ssd_norm_g': gain(ks[20], (DEPTH, SSD_WIDTH)),
        'w_out': nrm(ks[21], (DEPTH, D_MIX, D_MODEL), D_MIX),
    }

def reference(x, norm_g, w_in, q_a_norm, w_q_b, kv_a_norm, w_kv_b, q_norm, k_norm,
              conv_dw_w, conv_dw_b, conv_ln_g, conv_ln_b, conv_pw_w,
              ssd_conv_w, ssd_conv_b, ssd_dt_bias, ssd_A_log, ssd_D, ssd_norm_g, w_out):
    for i in range(DEPTH):
        x = hybrid_layer(x, norm_g[i], w_in[i], q_a_norm[i], w_q_b[i], kv_a_norm[i], w_kv_b[i],
                         q_norm[i], k_norm[i], conv_dw_w[i], conv_dw_b[i], conv_ln_g[i],
                         conv_ln_b[i], conv_pw_w[i], ssd_conv_w[i], ssd_conv_b[i],
                         ssd_dt_bias[i], ssd_A_log[i], ssd_D[i], ssd_norm_g[i], w_out[i])
    return x


_drawn_inputs = setup_inputs


def setup_inputs(seed=0):
    import zlib

    import numpy as np

    out = dict(_drawn_inputs(seed))
    spreads = {}
    factors = {'q_a_norm': 8.0,
     'kv_a_norm': 8.0,
     'q_norm': 8.0,
     'k_norm': 8.0,
     'conv_dw_b': 6.513,
     'conv_ln_g': 8.0,
     'conv_ln_b': 8.0,
     'ssd_conv_b': 2.691,
     'ssd_D': 7.408,
     'ssd_norm_g': 3.996}
    for name, (base, spread) in spreads.items():
        noise = np.random.default_rng([zlib.crc32(name.encode()), seed]).standard_normal(out[name].shape)
        drawn = base * np.exp(spread * noise) if base else spread * noise
        out[name] = __import__('jax').numpy.asarray(drawn.astype(out[name].dtype))
    for name, factor in factors.items():
        out[name] = (out[name] * factor).astype(out[name].dtype)
    return out
```

```python
from contextlib import ExitStack
import math

import numpy as np

import concourse.bass as bass
from concourse import mybir

F32 = mybir.dt.float32
F32R = mybir.dt.float32r
ALU = mybir.AluOpType
ACT = mybir.ActivationFunctionType
AX_X = mybir.AxisListType.X

P = 128
D_MODEL, SEQ, DEPTH = 2048, 512, 2
HEADS, NOPE, ROPE, VDIM = 6, 128, 64, 128
QK_HEAD = NOPE + ROPE
Q_LORA, KV_LORA = 512, 256
CONV_WIDTH, CONV_K = 512, 31
SSD_HEADS, SSD_P, SSD_N, SSD_K = 12, 64, 128, 4
SSD_WIDTH = SSD_HEADS * SSD_P
NORM_EPS, LN_EPS = 1e-6, 1e-5
ROPE_THETA = 10000.0
KX = D_MODEL // P
NT = SEQ // P
GH = SSD_HEADS // 2
SCALE = 1.0 / math.sqrt(QK_HEAD)

_OFF = dict(zip(("cq", "ckv", "kpe", "gmla", "uconv", "gconv", "z", "xbc", "dt"),
                np.cumsum([0, Q_LORA, KV_LORA, ROPE, HEADS * VDIM, 2 * CONV_WIDTH, CONV_WIDTH, SSD_WIDTH,
                           SSD_WIDTH + 4 * SSD_N]).tolist()))


def tiles_in():
    t = [("cq", j, [(_OFF["cq"] + P * j, P)]) for j in range(4)]
    t += [("ckv", j, [(_OFF["ckv"] + P * j, P)]) for j in range(2)]
    t += [("kpe", 0, [(_OFF["kpe"], ROPE), (_OFF["dt"], SSD_HEADS)])]
    t += [("gmla", j, [(_OFF["gmla"] + P * j, P)]) for j in range(6)]
    for j in range(4):
        t += [("ua", j, [(_OFF["uconv"] + P * j, P)]), ("ug", j, [(_OFF["uconv"] + CONV_WIDTH + P * j, P)])]
    for g in range(2):
        for i, c in enumerate([3 * g, 3 * g + 1, 3 * g + 2, 6 + g, 8 + g]):
            t += [("xbc", 5 * g + i, [(_OFF["xbc"] + P * c, P)])]
    t += [("gconv", j, [(_OFF["gconv"] + P * j, P)]) for j in range(4)]
    t += [("z", j, [(_OFF["z"] + P * j, P)]) for j in range(6)]
    return t


TILES = tiles_in()
XBC_CHANNELS = [3 * g + i if i < 3 else 6 + 2 * (i - 3) + g for g in range(2) for i in range(5)]


def hooks():
    h = {}

    def put(u, *task):
        h.setdefault(u, []).append(task)

    put(0, "rx")
    put(8, "cq_sum")
    put(12, "ckv_sum")
    put(13, "v", 0)
    put(14, "v", 1)
    put(15, "kd_turn")
    put(17, "acs")
    put(19, "acs_turn")
    for p in range(3):
        put(18 + 4 * p, "head_sum", p)
        put(19 + 4 * p, "head_apply", p, 0)
        put(20 + 4 * p, "head_apply", p, 1)
        put(21 + 4 * p, "rotate", p)
    for p in range(3):
        put(16 + 4 * p, "proj", p)
    for u in range(28, 54):
        put(u, "attend", u - 28)
    for s in range(8):
        put(54 + 2 * s, "ssd_a", s)
        put(56 + 2 * s, "ssd_b", s)
    for u in range(56, 70, 2):
        h[u].sort(reverse=True)
    put(71, "ln_mean")
    put(73, "ln_var")
    for f in range(4):
        put(77 + f, "pw", f)
    return h


def steps():
    s, units, hk = [], [], hooks()

    def unit(*what):
        units.append(what)
        return len(units) - 1

    for j in range(len(TILES)):
        for half in range(2):
            s.append(("in", (j, half), [unit("in", j, half)]))
            for name, *args in hk.get(2 * j + half, []):
                own = []
                if name == "v":
                    own = [unit("v", args[0])]
                if name == "proj":
                    own = [unit("qn", args[0]), unit("qrkn", args[0])]
                if name == "pw":
                    own = [unit("pw", args[0])]
                s.append((name, tuple(args), own))
    s.append(("ssd_sum", (), []))
    for f in range(KX):
        for half in range(2):
            s.append(("out", (f, half), [unit("out", f, half)]))
    return s, units


STEPS, UNITS = steps()


def finished_in_attention(j):
    return TILES[j][0] == "xbc" and j <= 25


def tile_columns(j):
    return sum(n for _, n in TILES[j][2])


def unit_width(what):
    if what[0] == "in":
        return 8 * tile_columns(what[1])
    return {"v": 2 * 3 * VDIM, "qn": 1024, "qrkn": 1024, "pw": 4 * P, "out": 1024}[what[0]]


WIDTHS = [unit_width(w) for w in UNITS]
STARTS = np.cumsum([0] + [P * w for w in WIDTHS]).tolist()
NU = len(UNITS)
TILE_UNIT = [UNITS.index(("in", j, 1)) for j in range(len(TILES))] + [UNITS.index(("out", f, 1)) for f in range(KX)]
STAGE, RING = 2, 3
assert NU % STAGE == 0 and NU % RING == 0

PARAM_COLS = {}
_at = 0
for _name, _n in (("norm_g", KX), ("qa", 4), ("kva", 2), ("qn", 1), ("qr", 1), ("kn", 1), ("kr", 1),
                  ("dww", 4 * CONV_K), ("dwb", 4), ("lng", 4), ("lnb", 4), ("scw", 10 * SSD_K), ("scb", 10),
                  ("skip", 6), ("sng", 6), ("dtb", SSD_HEADS), ("alog", SSD_HEADS)):
    PARAM_COLS[_name] = (_at, _n)
    _at += _n
NPAR = _at
ACT_CHAIN, DVE_CHAIN = 32, 358
NCONST = 2 * SEQ + 3 * P


class Signal:

    def __init__(self, nc, ctx, name, per_layer, credit=0):
        self.name, self.per_layer, self.credit, self.made = name, per_layer, credit, 0
        self.sem = ctx.enter_context(nc.semaphore(name))

    def at(self, layer, n):
        return layer * self.per_layer + (self.credit + n)

    def next(self, layer):
        self.made += 1
        return self.at(layer, self.made)


def hybrid_kernel(nc, x, weights, params, consts, out, acs_rows):
    ctx = ExitStack()
    with ctx:
        base = nc.sbuf_base
        base += -base % 64
        used = [base]

        def region(size):
            at = used[0]
            used[0] += size + (-size) % 32
            assert used[0] <= nc.sbuf_usable_end, used[0]
            return at

        def sb(name, shape, dt=F32, at=None):
            size = 4 * int(np.prod(shape[1:]))
            return nc.alloc_sbuf_tensor_at(name, shape, dt, offset=region(size) if at is None else at)

        def ps(name):
            return ctx.enter_context(nc.psum_tensor(name, [P, SEQ], F32))

        hhi = sb("hhi", [P, KX, SEQ], F32R)
        hlo = sb("hlo", [P, KX, SEQ], F32R)
        at_xg = region(4 * KX * SEQ)
        xg = sb("xg", [P, KX, SEQ], F32, at_xg)
        value = sb("value", [P, NT, HEADS * VDIM], F32, at_xg + 4 * 10 * SEQ)
        stage = [sb(f"stage{i}", [P, 1024]) for i in range(STAGE)]
        whi = [sb(f"whi{i}", [P, 1024], F32R) for i in range(RING)]
        wlo = [sb(f"wlo{i}", [P, 1024], F32R) for i in range(RING)]
        const = sb("const", [P, NCONST])
        cos, sin = const[:, 0:SEQ], const[:, SEQ:2 * SEQ]
        ident = const[:, 2 * SEQ:2 * SEQ + P]
        until = const[:, 2 * SEQ + P:2 * SEQ + 2 * P]
        mask = const[:, 2 * SEQ + 2 * P:2 * SEQ + 3 * P]
        ones = sb("ones", [P, P])
        eps_col = sb("eps_col", [P, 2])
        pv = sb("pv", [P, NPAR])
        rx = sb("rx", [P, SEQ])
        rcq = sb("rcq", [P, SEQ])
        rckv = sb("rckv", [P, SEQ])
        temp = sb("temp", [P, SEQ])
        temp2 = sb("temp2", [P, SEQ])
        small = sb("small", [P, 6, 48])
        cols = sb("cols", [P, 32])

        m1 = region(8704 + 8192)
        cqhi = sb("cqhi", [P, 4, SEQ], F32R, m1)
        cqlo = sb("cqlo", [P, 4, SEQ], F32R, m1 + 8192)
        PADC = CONV_K - 1
        glu = sb("glu", [P, 4, PADC + SEQ], F32, m1)
        cacc = sb("cacc", [P, 4, SEQ], F32, m1 + 8704)
        pwhi = sb("pwhi", [P, 4, SEQ], F32R, m1)
        pwlo = sb("pwlo", [P, 4, SEQ], F32R, m1 + 8704)
        m2 = region(8256)
        ckvhi = sb("ckvhi", [P, 2, SEQ], F32R, m2)
        ckvlo = sb("ckvlo", [P, 2, SEQ], F32R, m2 + 4096)
        key2 = sb("key2", [P, 3, SEQ], F32, m2)
        ecs = sb("ecs", [P, GH, P], F32, m2)
        cbm = sb("cbm", [P, P], F32, m2 + 3072)
        raw = sb("raw", [P, 3 + SEQ], F32, m2 + 6144)
        m3 = region(12288)
        m4 = region(12288)
        qk = [sb("qk0", [P, 6, SEQ], F32, m3), sb("qk1", [P, 6, SEQ], F32, m4)]
        QK = [[qk[p][:, i, :] for i in range(6)] for p in range(2)]
        QK.append([xg[:, 6 + i, :] for i in range(3)] + [key2[:, i, :] for i in range(3)])
        xb = [sb("xb0", [P, 5, SEQ], F32, m4), sb("xb1", [P, 5, SEQ], F32, m3)]
        xdt = sb("xdt", [P, GH * SSD_P], F32, m3 + 10240)
        btok = sb("btok", [P, P], F32, m3 + 10240 + 1536)
        xw = sb("xw", [P, GH * SSD_P], F32, m4 + 10240)
        kr2 = sb("kr2", [P, SEQ])
        sqkp = sb("sqkp", [P, SEQ])
        e0 = region(8192)
        sqh = sb("sqh", [P, 4, SEQ], F32, e0)
        sqc, sqkv, kd, sqx = sqh[:, 0, :], sqh[:, 1, :], sqh[:, 2, :], sqh[:, 3, :]
        acs48 = sb("acs48", [48, P])[:, :]
        pvn = sb("pvn", [P, NPAR], F32, e0 + 4096)
        prob = [sb(f"prob{i}", [P, SEQ], F32, e0 + 2048 * i) for i in range(2)]
        probT = [sb(f"probT{i}", [P, SEQ], F32, e0 + 4096 + 2048 * i) for i in range(2)]
        acsb = sb("acsb", [P, GH, P], F32, e0)
        mt = sb("mt", [P, GH, P], F32, e0 + 3072)
        state = sb("state", [P, GH * SSD_P], F32, e0 + 6144)
        xr = [sb(f"xr{i}", [P, SEQ], F32, e0 + 2048 * i) for i in range(2)]
        sqz, csum = kr2, sqkp

        dt48, da48, acst = small[:, 0, :], small[:, 1, :], small[:, 2, :]
        sa, sbb, scc = small[:, 3, :], small[:, 4, :], small[:, 5, :]
        rkc, rmax, negm, rsum, rinv = cols[:, 0:4], cols[:, 4:5], cols[:, 5:6], cols[:, 6:7], cols[:, 7:8]
        dte, cd = cols[:, 8:14], cols[:, 14:20]
        aneg = cols[:, 20:32]

        acc = [ps("acc0"), ps("acc1")]
        S = [ps("S0"), ps("S1")]
        T = [ps("T0"), ps("T1")]
        M, O = ps("M"), ps("O")

        def par(name, i=0, n=1):
            at = PARAM_COLS[name][0] + i
            return pv[:, at:at + n]

        def sig(name, per_layer, credit=0):
            return Signal(nc, ctx, name, per_layer, credit)

        first_set, first_sq, first_added, pool_go = (ctx.enter_context(nc.semaphore(n))
                                                     for n in ("first_set", "first_sq", "first_added", "pool_go"))

        stage_loaded = [sig(f"stage_loaded{i}", 16 * (NU // STAGE)) for i in range(STAGE)]
        x_loaded = [sig(f"x_loaded{i}", 0) for i in range(4)]
        const_loaded = sig("const_loaded", 0)
        out_copied = sig("out_copied", 0)
        params_loaded = sig("params_loaded", 16, credit=16)
        acs_stored = sig("acs_stored", 16)
        acsb_loaded = sig("acsb_loaded", 16 * 8)
        res_loaded = [sig(f"res_loaded{i}", 16 * KX // 2) for i in range(2)]
        x_stored = sig("x_stored", 16 * KX)
        x_free = sig("x_free", 1, credit=1)

        unit_used = sig("unit_used", NU, credit=RING)
        hi_done = sig("hi_done", NU)
        lo_done = sig("lo_done", NU, credit=STAGE)
        params_ready = sig("params_ready", 1)
        x_ready = sig("x_ready", KX, credit=KX)
        h_hi = sig("h_hi", 2 * KX)
        h_lo = sig("h_lo", 2 * KX)
        acc_taken = sig("acc_taken", len(TILES) + KX)
        rx_sum = sig("rx_sum", 1)
        rx_ready = sig("rx_ready", 1)
        sqx_ready = sig("sqx_ready", 1, credit=1)
        cq_hi = sig("cq_hi", 6)
        lat_lo = sig("lat_lo", 6)
        lat_sq = sig("lat_sq", 6)
        lat_sum = sig("lat_sum", 2)
        lat_r = sig("lat_r", 2)
        tanh_done = sig("tanh_done", 6 + 4 + 10 + 4 + 6 + 4)
        tanh_in = sig("tanh_in", 6 + 4 + 10 + 4 + 6 + 4)
        kd_ready = sig("kd_ready", 1)
        kd_turned = sig("kd_turned", 1)
        kr_half = sig("kr_half", 1)
        kr_both = sig("kr_both", 1)
        dt_asked = sig("dt_asked", 1)
        dt_exp = sig("dt_exp", 1)
        da_ready = sig("da_ready", 1)
        acs_sum = sig("acs_sum", 1)
        acs_ready = sig("acs_ready", 1)
        acs_turned = sig("acs_turned", 1)
        acs48_ready = sig("acs48_ready", 1)
        v_done = sig("v_done", 6)
        v_taken = sig("v_taken", 8)
        proj_done = sig("proj_done", 12)
        proj_taken = sig("proj_taken", 15)
        sq_part = sig("sq_part", 3)
        sq_ready = sig("sq_ready", 3)
        head_sum = sig("head_sum", 12)
        head_r = sig("head_r", 12)
        qk_ready = sig("qk_ready", 3)
        scores_done = sig("scores_done", 24)
        max_ready = sig("max_ready", 24)
        exp_done = sig("exp_done", 24)
        rinv_ready = sig("rinv_ready", 24)
        prob_ready = sig("prob_ready", 24)
        probT_done = sig("probT_done", 24)
        probT_taken = sig("probT_taken", 24)
        o_done = sig("o_done", 24)
        o_taken = sig("o_taken", 24)
        tap3_done = sig("tap3_done", 10)
        xb_ready = sig("xb_ready", 10)
        ssd_turned = sig("ssd_turned", 8)
        dte_in = sig("dte_in", 8)
        dte_exp = sig("dte_exp", 8)
        ecs_exp = sig("ecs_exp", 8)
        seg_in = sig("seg_in", 8)
        seg_exp = sig("seg_exp", 8)
        ssd_in = sig("ssd_in", 8)
        ssd_y = sig("ssd_y", 8)
        ssd_taken = sig("ssd_taken", 8)
        conv_sum_in = sig("conv_sum_in", 2)
        conv_sum = sig("conv_sum", 2)
        conv_r = sig("conv_r", 1)
        pw_in = sig("pw_in", 4)
        pw_hi = sig("pw_hi", 4)
        pw_lo = sig("pw_lo", 4)
        pw_taken = sig("pw_taken", 4)
        ssd_sq = sig("ssd_sq", 1)
        ssd_sum = sig("ssd_sum", 1)
        ssd_r = sig("ssd_r", 1)
        branch_ready = sig("branch_ready", 6)
        tap_done = sig("tap_done", 4 * CONV_K)
        act_chain = sig("act_chain", ACT_CHAIN)
        dve_chain = sig("dve_chain", DVE_CHAIN)

        block = ctx.enter_context(nc.Block())

        @block.sync
        def _(sp):
            for i in range(4):
                sp.dma_start(xg[:, 4 * i:4 * i + 4, :], x[:, 4 * i * SEQ:(4 * i + 4) * SEQ]
                                            .rearrange("p (k t) -> p k t", k=4)).then_inc(x_loaded[i].sem, 16)
                if i == 0:
                    sp.dma_start(const[:, :], consts).then_inc(const_loaded.sem, 16)
                    sp.dma_start(pvn[:, :], params[0:P, :]).then_inc(params_loaded.sem, 16)
            with sp.Fori(0, DEPTH) as layer:
                for name, args, own in STEPS:
                    for u in own:
                        sp.wait_ge(lo_done.sem, lo_done.at(layer, u - STAGE + 1))
                        src = weights[bass.ds(layer, 1), STARTS[u]:STARTS[u + 1]].rearrange("o (p w) -> (o p) w", p=P)
                        sp.dma_start(stage[u % STAGE][:, 0:WIDTHS[u]], src).then_inc(stage_loaded[u % STAGE].sem, 16)
                    if name == "out" and args == (1, 0):
                        sp.wait_ge(ssd_taken.sem, ssd_taken.at(layer, 8))
                        sp.dma_start(pvn[:, :], params[bass.ds(layer * P + P, P), :]).then_inc(params_loaded.sem, 16)
            sp.wait_ge(params_loaded.sem, params_loaded.at(DEPTH, 0))

        @block.gpsimd
        def _(pool):
            pool.sem_inc(x_free.sem, 1)

            def go():
                pool.sem_inc(pool_go, 1)

            for i in range(8):
                pool.wait_ge(unit_used.sem, unit_used.at(0, 1 + i))
                go()
                pool.dma_start(out[:, 2 * i * SEQ:(2 * i + 2) * SEQ],
                               x[:, 2 * i * SEQ:(2 * i + 2) * SEQ]).then_inc(out_copied.sem, 16)
                pool.wait_ge(out_copied.sem, 16 * (i + 1))

            with pool.Fori(0, DEPTH) as layer:
                for name, args, own in STEPS:
                    if name == "acs_turn":
                        pool.wait_ge(acs48_ready.sem, acs48_ready.at(layer, 1))
                        go()
                        pool.dma_start(acs_rows, acs48).then_inc(acs_stored.sem, 16)
                        pool.wait_ge(acs_stored.sem, acs_stored.at(layer, 16))
                    if name == "ssd_a":
                        s = args[0]
                        g, c = s // NT, s % NT
                        if s == 0:
                            pool.wait_ge(o_taken.sem, o_taken.at(layer, 24))
                        else:
                            pool.wait_ge(ssd_in.sem, ssd_in.at(layer, s))
                        rows = acs_rows[12 * c + 6 * g:12 * c + 6 * g + 6, :].rearrange("(o h) l -> o (h l)", o=1)
                        go()
                        pool.dma_start(acsb[:, :, :].rearrange("p h l -> p (h l)"),
                                                      rows.to_broadcast([P, GH * P])).then_inc(acsb_loaded.sem, 16)
                    if name == "out" and args[1] == 0:
                        f = args[0]
                        if f == 0:
                            pool.wait_ge(ssd_taken.sem, ssd_taken.at(layer, 8))
                        if f >= 2:
                            pool.wait_ge(acc_taken.sem, acc_taken.at(layer, len(TILES) + f - 1))
                        go()
                        pool.dma_start(xr[f % 2][:, :], out[:, f * SEQ:(f + 1) * SEQ]).then_inc(res_loaded[f % 2].sem, 16)
                        if f >= 1:
                            pool.wait_ge(x_ready.sem, x_ready.at(layer, f))
                            go()
                            pool.dma_start(out[:, (f - 1) * SEQ:f * SEQ], xg[:, f - 1, :]).then_inc(x_stored.sem, 16)
                pool.wait_ge(x_ready.sem, x_ready.at(layer, KX))
                go()
                pool.dma_start(out[:, (KX - 1) * SEQ:KX * SEQ], xg[:, KX - 1, :]).then_inc(x_stored.sem, 16)
                pool.wait_ge(x_stored.sem, x_stored.at(layer, 16 * KX))
                pool.sem_inc(x_free.sem, 1)
        @block.tensor
        def _(pe):
            def three(out, a, b, c, d, start, stop):
                nc.tensor.matmul(out, a, c, start=start, stop=False)
                nc.tensor.matmul(out, a, d, start=False, stop=False)
                return nc.tensor.matmul(out, b, c, start=False, stop=stop)

            def full(out, a, b, start=True, stop=True):
                return nc.tensor.matmul(out, a, b, start=start, stop=stop)

            def w(u, at, n):
                return whi[u % RING][:, at:at + n], wlo[u % RING][:, at:at + n]

            pe.sem_inc(unit_used.sem, RING)
            pe.wait_ge(const_loaded.sem, 16)
            with pe.Fori(0, DEPTH) as layer:
                def total(signal, parts, bank):
                    last = None
                    for i, part in enumerate(parts):
                        last = full(bank[:, :], ones[:, :], part, i == 0, i == len(parts) - 1)
                    last.then_inc(signal.sem, 1)

                for name, args, own in STEPS:
                    for u in own:
                        pe.wait_ge(lo_done.sem, lo_done.at(layer, u + 1))
                    if name == "in":
                        j, half = args
                        u, m = own[0], tile_columns(j)
                        if half == 0 and j >= 2:
                            pe.wait_ge(acc_taken.sem, acc_taken.at(layer, j - 1))
                        for k8 in range(8):
                            k = 8 * half + k8
                            if j == 0:
                                pe.wait_ge(h_lo.sem, h_lo.at(layer, k + 1))
                            last = three(acc[j % 2][0:m, :], *w(u, k8 * m, m), hhi[:, k, :], hlo[:, k, :],
                                         k == 0, k == KX - 1)
                        last.then_inc(unit_used.sem, 1)
                    elif name == "rx":
                        pe.wait_ge(sqx_ready.sem, sqx_ready.at(layer, 0))
                        total(rx_sum, [sqx], M)
                    elif name == "cq_sum":
                        pe.wait_ge(rx_ready.sem, rx_ready.at(layer, 1))
                        pe.wait_ge(lat_sq.sem, lat_sq.at(layer, 4))
                        total(lat_sum, [sqc], M)
                    elif name == "ckv_sum":
                        pe.wait_ge(lat_r.sem, lat_r.at(layer, 1))
                        pe.wait_ge(lat_sq.sem, lat_sq.at(layer, 6))
                        full(M[:, :], ones[:, :], sqkv)
                        for t in range(NT):
                            last = full(O[:, t:t + 1], sqkv[:, t * P:(t + 1) * P], ones[:, 0:1])
                        last.then_inc(lat_sum.sem, 1)
                    elif name == "kd_turn":
                        pe.wait_ge(kd_ready.sem, kd_ready.at(layer, 1))
                        pe.wait_ge(v_taken.sem, v_taken.at(layer, 8))
                        for c in range(NT):
                            last = nc.tensor.transpose(T[0][:, c * P:(c + 1) * P], kd[:, c * P:(c + 1) * P], ident)
                        last.then_inc(kd_turned.sem, 1)
                    elif name == "acs":
                        pe.wait_ge(da_ready.sem, da_ready.at(layer, 1))
                        full(O[:, 16:64], until, da48).then_inc(acs_sum.sem, 1)
                    elif name == "acs_turn":
                        pe.wait_ge(acs_ready.sem, acs_ready.at(layer, 1))
                        wide = small[:, :, :].rearrange("p a b -> p (a b)")[:, 96:96 + P]
                        nc.tensor.transpose(O[:, P:2 * P], wide, ident).then_inc(acs_turned.sem, 1)
                    elif name == "v":
                        hf, u = args[0], own[0]
                        if hf == 0:
                            pe.wait_ge(lat_lo.sem, lat_lo.at(layer, 6))
                            pe.wait_ge(lat_r.sem, lat_r.at(layer, 2))
                        for t in range(NT):
                            bank = (S + T)[t]
                            if hf:
                                pe.wait_ge(v_taken.sem, v_taken.at(layer, t + 1))
                            for k in range(2):
                                wh, wl = w(u, k * 384, 384)
                                last = three(bank[:, 0:384], ckvhi[:, k, t * P:(t + 1) * P],
                                             ckvlo[:, k, t * P:(t + 1) * P], wh, wl, k == 0, k == 1)
                            if t < NT - 1:
                                last.then_inc(v_done.sem, 1)
                        last.then_inc(unit_used.sem, 1)
                    elif name == "proj":
                        p = args[0]
                        if p == 0:
                            pe.wait_ge(dt_asked.sem, dt_asked.at(layer, 1))
                        else:
                            pe.wait_ge(head_r.sem, head_r.at(layer, 4 * p))
                        ua, ub = own
                        for i in range(5):
                            bank = (S + T + [M])[i]
                            kk = 4 if i < 3 else 2
                            for k in range(kk):
                                if i < 2:
                                    ww = w(ua, (4 * i + k) * P, P)
                                elif i == 2:
                                    ww = w(ub, k * P, P)
                                else:
                                    ww = w(ub, (4 + 2 * (i - 3) + k) * P, P)
                                hi, lo = (cqhi, cqlo) if i < 3 else (ckvhi, ckvlo)
                                last = three(bank[:, :], *ww, hi[:, k, :], lo[:, k, :], k == 0, k == kk - 1)
                            if i < 4:
                                last.then_inc(proj_done.sem, 1)
                        last.then_inc(unit_used.sem, 2)
                    elif name == "head_sum":
                        p = args[0]
                        pe.wait_ge(sq_ready.sem, sq_ready.at(layer, p + 1))
                        for i in range(4):
                            full((S + T)[i][:, :], ones[:, :], sqh[:, i, :]).then_inc(head_sum.sem, 1)
                    elif name == "attend":
                        n = args[0]
                        if n < 24:
                            p, h, qb = n // 8, n // 4 % 2, n % 4
                            q, width = slice(qb * P, qb * P + P), (qb + 1) * P
                            pe.wait_ge(qk_ready.sem, qk_ready.at(layer, p + 1))
                            if n < 2:
                                pe.wait_ge(head_r.sem, head_r.at(layer, 12))
                            else:
                                pe.wait_ge(exp_done.sem, exp_done.at(layer, n - 1))
                            r = slice(64 * h, 64 * h + 64)
                            full(S[n % 2][:, 0:width], QK[p][h][:, q], QK[p][3 + h][:, 0:width], True, False)
                            full(S[n % 2][:, 0:width], QK[p][2][r, q], QK[p][5][r, 0:width], False, True).then_inc(scores_done.sem, 1)
                        if 1 <= n <= 24:
                            m = n - 1
                            pe.wait_ge(prob_ready.sem, prob_ready.at(layer, m + 1))
                            if m >= 2:
                                pe.wait_ge(probT_taken.sem, probT_taken.at(layer, m - 1))
                            for kb in range(m % 4 + 1):
                                b = slice(kb * P, kb * P + P)
                                last = nc.tensor.transpose(T[m % 2][:, b], prob[m % 2][:, b], ident)
                            last.then_inc(probT_done.sem, 1)
                        if 2 <= n:
                            m = n - 2
                            qb, hh = m % 4, m // 4
                            pe.wait_ge(probT_taken.sem, probT_taken.at(layer, m + 1))
                            if m == 0:
                                pe.wait_ge(acs48_ready.sem, acs48_ready.at(layer, 1))
                            else:
                                pe.wait_ge(o_taken.sem, o_taken.at(layer, m))
                            for kb in range(qb + 1):
                                last = full(O[:, qb * P:(qb + 1) * P], value[:, kb, hh * P:(hh + 1) * P],
                                            probT[m % 2][:, kb * P:(kb + 1) * P], kb == 0, kb == qb)
                            last.then_inc(o_done.sem, 1)
                    elif name == "ssd_a":
                        s = args[0]
                        g, c = s // NT, s % NT
                        pe.wait_ge(xb_ready.sem, xb_ready.at(layer, 5 * g + 5))
                        if s == 0:
                            pe.wait_ge(probT_taken.sem, probT_taken.at(layer, 24))
                        else:
                            pe.wait_ge(ssd_in.sem, ssd_in.at(layer, s))
                        b = slice(c * P, c * P + P)
                        for i in range(4):
                            nc.tensor.transpose(T[0][:, i * P:(i + 1) * P], xb[g][:, i, b], ident)
                        full(T[1][:, 0:P], xb[g][:, 3, b], xb[g][:, 4, b]).then_inc(ssd_turned.sem, 1)
                    elif name == "ssd_b":
                        s = args[0]
                        g, c = s // NT, s % NT
                        pe.wait_ge(ssd_in.sem, ssd_in.at(layer, s + 1))
                        if s == 0:
                            pe.wait_ge(exp_done.sem, exp_done.at(layer, 24))
                        else:
                            pe.wait_ge(ssd_taken.sem, ssd_taken.at(layer, s))
                        for h in range(GH):
                            o = S[0][64 * (h % 2):64 * (h % 2) + 64, (h // 2) * P:(h // 2 + 1) * P]
                            hp = slice(h * SSD_P, (h + 1) * SSD_P)
                            last = full(o, xdt[:, hp], mt[:, h, :], True, c == 0)
                            if c:
                                last = full(o, state[:, hp], ecs[:, h, :], False, True)
                        if c < NT - 1:
                            last = full(S[1][:, 0:GH * SSD_P], btok[:, :], xw[:, :])
                        last.then_inc(ssd_y.sem, 1)
                    elif name == "ln_mean":
                        pe.wait_ge(conv_sum_in.sem, conv_sum_in.at(layer, 1))
                        pe.wait_ge(proj_taken.sem, proj_taken.at(layer, 15))
                        total(conv_sum, [csum[:, :]], M)
                    elif name == "ln_var":
                        pe.wait_ge(conv_sum_in.sem, conv_sum_in.at(layer, 2))
                        total(conv_sum, [csum[:, :]], M)
                    elif name == "pw":
                        f, u = args[0], own[0]
                        bank = [O, M][f % 2]
                        if f == 0:
                            pe.wait_ge(o_taken.sem, o_taken.at(layer, 24))
                            pe.wait_ge(conv_r.sem, conv_r.at(layer, 1))
                        if f >= 2:
                            pe.wait_ge(pw_taken.sem, pw_taken.at(layer, f - 1))
                        for k in range(4):
                            pe.wait_ge(pw_lo.sem, pw_lo.at(layer, k + 1))
                            last = three(bank[:, :], *w(u, k * P, P), pwhi[:, k, :], pwlo[:, k, :], k == 0, k == 3)
                        last.then_inc(unit_used.sem, 1)
                    elif name == "out":
                        f, half = args
                        u, a = own[0], acc[(f + 1) % 2]
                        if half == 0:
                            pe.wait_ge(acc_taken.sem, acc_taken.at(layer, len(TILES) + f - 1))
                        for k8 in range(8):
                            i = 8 * half + k8
                            k = i
                            if f == 0:
                                if k == 5:
                                    pe.wait_ge(ssd_sq.sem, ssd_sq.at(layer, 1))
                                    pe.wait_ge(pw_taken.sem, pw_taken.at(layer, 4))
                                    total(ssd_sum, [sqz[:, :]], M)
                                pe.wait_ge(h_lo.sem, h_lo.at(layer, KX + i + 1))
                            last = three(a[:, :], *w(u, k8 * P, P), hhi[:, k, :], hlo[:, k, :], i == 0, i == KX - 1)
                        last.then_inc(unit_used.sem, 1)

        @block.scalar
        def _(act):
            act.wait_ge(const_loaded.sem, 16)
            for i in range(4):
                act.wait_ge(x_loaded[i].sem, 16)
                for k in range(4 * i, 4 * i + 4):
                    t = [temp, temp2][k % 2]
                    if k >= 2:
                        act.wait_ge(first_added, k - 1)
                    nc.scalar.activation(t[:, :], xg[:, k, :], ACT.Square).then_inc(first_sq, 1)
            with act.Fori(0, DEPTH) as layer:
                def a(signal, out, in_, func, **more):
                    signal = signal or act_chain
                    nc.scalar.activation(out, in_, func, **more).then_inc(signal.sem, 1)
                    act.wait_ge(signal.sem, signal.next(layer))

                def split(u):
                    if u >= NU:
                        return
                    act.wait_ge(stage_loaded[u % STAGE].sem, stage_loaded[u % STAGE].at(layer, 16 * (u // STAGE + 1)))
                    act.wait_ge(unit_used.sem, unit_used.at(layer, u - RING + 1))
                    w = WIDTHS[u]
                    nc.scalar.activation(whi[u % RING][:, 0:w], stage[u % STAGE][:, 0:w], ACT.Copy).then_inc(hi_done.sem, 1)

                def rsqrt(signal, out, total, n, eps, turn=None):
                    a(None, out, total, ACT.Ln, scale=1.0 / n, bias=eps_col[0:out.shape[0], eps:eps + 1])
                    a(signal, out, out, ACT.Exp, scale=-0.5)

                act.wait_ge(params_loaded.sem, params_loaded.at(layer, 0))
                a(params_ready, pv[:, :], pvn[:, :], ACT.Copy)
                for u in range(RING - 1):
                    split(u)
                act.wait_ge(x_ready.sem, x_ready.at(layer, 0))
                for k in range(KX):
                    if k == 6:
                        split(RING - 1)
                    nc.scalar.activation(hhi[:, k, :], xg[:, k, :], ACT.Identity, scale=par("norm_g", k)).then_inc(h_hi.sem, 1)

                tanhs = [0]

                def tanh(scale=1.0, src=None):
                    tanhs[0] += 1
                    act.wait_ge(tanh_in.sem, tanh_in.at(layer, tanhs[0]))
                    a(tanh_done, temp2[:, :], temp[:, :] if src is None else src, ACT.Tanh, scale=scale)

                for name, args, own in STEPS:
                    for u in own:
                        split(u + RING)
                    if name == "in" and args[1] == 1:
                        kind, i, _ = TILES[args[0]]
                        if kind in ("cq", "ckv"):
                            act.wait_ge(acc_taken.sem, acc_taken.at(layer, args[0] + 1))
                            hi, g = (cqhi, "qa") if kind == "cq" else (ckvhi, "kva")
                            nc.scalar.activation(hi[:, i, :], temp[:, :], ACT.Identity, scale=par(g, i)).then_inc(cq_hi.sem, 1)
                        if kind == "kpe":
                            act.wait_ge(kr_half.sem, kr_half.at(layer, 1))
                            a(kr_both, kr2[64:128, :], kr2[0:64, :], ACT.Copy)
                        if kind in ("gmla", "ug", "gconv", "z"):
                            tanh()
                        if kind == "xbc":
                            ch = XBC_CHANNELS[i]
                            act.wait_ge(acc_taken.sem, acc_taken.at(layer, args[0] + 1))
                            nc.scalar.activation(xb[i // 5][:, i % 5, :], raw[:, 3:3 + SEQ], ACT.Identity,
                                                 scale=par("scw", SSD_K * ch + 3),
                                                 bias=par("scb", ch)).then_inc(tap3_done.sem, 1)
                            if not finished_in_attention(args[0]):
                                tanh(1.0, xb[i // 5][:, i % 5, :])
                    elif name == "rx":
                        act.wait_ge(rx_sum.sem, rx_sum.at(layer, 1))
                        rsqrt(rx_ready, rx[:, :], M[:, :], D_MODEL, 0)
                    elif name == "cq_sum":
                        act.wait_ge(lat_sum.sem, lat_sum.at(layer, 1))
                        rsqrt(lat_r, rcq[:, :], M[:, :], Q_LORA, 0)
                    elif name == "ckv_sum":
                        act.wait_ge(lat_sum.sem, lat_sum.at(layer, 2))
                        rsqrt(None, rkc, O[:, 0:4], KV_LORA, 0)
                        rsqrt(lat_r, rckv[:, :], M[:, :], KV_LORA, 0)
                    elif name == "kd_turn":
                        act.wait_ge(dt_asked.sem, dt_asked.at(layer, 1))
                        a(None, aneg, par("alog", 0, SSD_HEADS), ACT.Exp)
                        a(dt_exp, sbb, sbb, ACT.Exp, scale=-1.0)
                    elif name == "acs":
                        act.wait_ge(acs_sum.sem, acs_sum.at(layer, 1))
                        a(acs_ready, acst, O[:, 16:64], ACT.Copy)
                    elif name == "acs_turn":
                        act.wait_ge(acs_turned.sem, acs_turned.at(layer, 1))
                        a(acs48_ready, acs48, O[0:48, P:2 * P], ACT.Copy)
                    elif name == "v":
                        hf = args[0]
                        for t in range(NT):
                            if t < NT - 1:
                                act.wait_ge(v_done.sem, v_done.at(layer, (NT - 1) * hf + t + 1))
                            else:
                                act.wait_ge(unit_used.sem, unit_used.at(layer, own[0] + 1))
                            nc.scalar.activation(value[:, t, 384 * hf:384 * hf + 384], (S + T)[t][:, 0:384],
                                                            ACT.Identity, scale=rkc[:, t:t + 1]).then_inc(v_taken.sem, 1)
                    elif name == "proj":
                        p = args[0]
                        for n, (i, to) in enumerate([(0, sqh[:, 0, :]), (1, sqh[:, 1, :]), (2, temp2[:, :]),
                                                     (3, sqh[:, 2, :]), (4, sqh[:, 3, :])]):
                            act.wait_ge(proj_taken.sem, proj_taken.at(layer, 5 * p + i + 1))
                            a(sq_part if n == 4 else None, to, QK[p][i], ACT.Square)
                    elif name == "head_sum":
                        p = args[0]
                        for i in range(4):
                            act.wait_ge(head_sum.sem, head_sum.at(layer, 4 * p + i + 1))
                            a(None, sqh[:, i, :], (S + T)[i][:, :], ACT.Ln, scale=1.0 / QK_HEAD, bias=eps_col[:, 0:1])
                        for i in range(4):
                            a(head_r, sqh[:, i, :], sqh[:, i, :], ACT.Exp, scale=-0.5)
                    elif name == "attend":
                        n = args[0]
                        if n < 24:
                            width = (n % 4 + 1) * P
                            act.wait_ge(max_ready.sem, max_ready.at(layer, n + 1))
                            if n >= 2:
                                act.wait_ge(probT_done.sem, probT_done.at(layer, n - 1))
                            a(exp_done, prob[n % 2][:, 0:width], S[n % 2][:, 0:width], ACT.Exp, scale=SCALE,
                              bias=negm, accum_out=rsum)
                        if 1 <= n <= 24:
                            m = n - 1
                            width = (m % 4 + 1) * P
                            act.wait_ge(probT_done.sem, probT_done.at(layer, m + 1))
                            if m >= 2:
                                act.wait_ge(o_done.sem, o_done.at(layer, m - 1))
                            nc.scalar.activation(probT[m % 2][:, 0:width], T[m % 2][:, 0:width], ACT.Copy).then_inc(probT_taken.sem, 1)
                        if n < 24:
                            width = (n % 4 + 1) * P
                            act.wait_ge(rinv_ready.sem, rinv_ready.at(layer, n + 1))
                            a(prob_ready, prob[n % 2][:, 0:width], prob[n % 2][:, 0:width], ACT.Copy, scale=rinv)
                        if n % 2 == 1 and finished_in_attention((n + 27) // 2):
                            i = TILES[(n + 27) // 2][1]
                            tanh(1.0, xb[i // 5][:, i % 5, :])
                    elif name == "ssd_a":
                        s = args[0]
                        act.wait_ge(acsb_loaded.sem, acsb_loaded.at(layer, 16 * (s + 1)))
                        if s:
                            act.wait_ge(ssd_y.sem, ssd_y.at(layer, s))
                        act.wait_ge(dte_in.sem, dte_in.at(layer, s + 1))
                        a(dte_exp, dte, dte, ACT.Exp)
                        a(ecs_exp, ecs[:, :, :], acsb[:, :, :], ACT.Exp)
                        act.wait_ge(seg_in.sem, seg_in.at(layer, s + 1))
                        a(seg_exp, mt[:, :, :], mt[:, :, :], ACT.Exp)
                    elif name == "ln_var":
                        act.wait_ge(conv_sum.sem, conv_sum.at(layer, 2))
                        rsqrt(conv_r, rckv[:, :], M[:, :], CONV_WIDTH, 1)
                        for j in range(4):
                            tanh()
                            act.wait_ge(pw_in.sem, pw_in.at(layer, j + 1))
                            a(pw_hi, pwhi[:, j, :], cacc[:, j, :], ACT.Copy)
                    elif name == "ssd_sum":
                        act.wait_ge(unit_used.sem, unit_used.at(layer, TILE_UNIT[len(TILES) - 1] + 1))
                        act.wait_ge(pw_taken.sem, pw_taken.at(layer, 4))
                        for k in range(KX):
                            if k == 8:
                                act.wait_ge(ssd_sum.sem, ssd_sum.at(layer, 1))
                                rsqrt(ssd_r, rcq[:, :], M[:, :], SSD_WIDTH, 0)
                            if k >= 10:
                                act.wait_ge(branch_ready.sem, branch_ready.at(layer, k - 9))
                            nc.scalar.activation(hhi[:, k, :], xg[:, k, :], ACT.Copy).then_inc(h_hi.sem, 1)

        @block.vector
        def _(dve):
            nc.vector.memset(ones[:, :], 1.0).then_inc(first_set, 1)
            nc.vector.memset(eps_col[:, 0:1], NORM_EPS).then_inc(first_set, 1)
            nc.vector.memset(eps_col[:, 1:2], LN_EPS).then_inc(first_set, 1)
            dve.sem_inc(lo_done.sem, STAGE)
            dve.wait_ge(const_loaded.sem, 16)
            dve.wait_ge(first_set, 3)
            for k in range(KX):
                dve.wait_ge(first_sq, k + 1)
                t = [temp, temp2][k % 2]
                if k == 0:
                    nc.vector.tensor_copy(sqx, t[:, :]).then_inc(first_added, 1)
                else:
                    dve.wait_ge(first_added, k)
                    nc.vector.tensor_tensor(sqx, sqx, t[:, :], ALU.add).then_inc(first_added, 1)
            dve.wait_ge(first_added, KX)
            dve.sem_inc(x_ready.sem, KX)
            dve.sem_inc(sqx_ready.sem, 1)

            with dve.Fori(0, DEPTH) as layer:
                def d(signal, ins, go=False):
                    signal = signal or dve_chain
                    ins.then_inc(signal.sem, 1)
                    value = signal.next(layer)
                    if not go:
                        dve.wait_ge(signal.sem, value)

                def mark(signal):
                    dve.sem_inc(signal.sem, 1)
                    signal.made += 1

                def tt(signal, out, x, y, op, go=False):
                    d(signal, nc.vector.tensor_tensor(out, x, y, op), go)

                def ts(signal, out, x, s1, op0, s2=None, op1=None, go=False):
                    if op1 is None:
                        d(signal, nc.vector.tensor_scalar(out, x, s1, None, op0), go)
                    else:
                        d(signal, nc.vector.tensor_scalar(out, x, s1, s2, op0, op1), go)

                def stt(signal, out, x, s, y, op0, op1, go=False):
                    d(signal, nc.vector.scalar_tensor_tensor(out=out, in0=x, scalar=s, in1=y, op0=op0, op1=op1), go)

                def split(u):
                    if u >= NU:
                        return
                    dve.wait_ge(hi_done.sem, hi_done.at(layer, u + 1))
                    w = WIDTHS[u]
                    nc.vector.tensor_tensor(wlo[u % RING][:, 0:w], stage[u % STAGE][:, 0:w],
                                                       whi[u % RING][:, 0:w].bitcast(F32), ALU.subtract).then_inc(lo_done.sem, 1)

                tanhs = [0]

                def silu(signal, out, y):
                    if taps_open[0]:
                        convolve(1)
                    tanhs[0] += 1
                    dve.wait_ge(tanh_done.sem, tanh_done.at(layer, tanhs[0]))
                    stt(signal, out, temp2[:, :], 1.0, y, ALU.add, ALU.mult)

                def evac(j, out, half=False, rows=P):
                    dve.wait_ge(unit_used.sem, unit_used.at(layer, TILE_UNIT[j] + 1))
                    if j == 0:
                        dve.wait_ge(rx_ready.sem, rx_ready.at(layer, 1))
                        dve.wait_ge(x_free.sem, x_free.at(layer, 0))
                    if half:
                        stt(acc_taken, out, acc[j % 2][0:rows, :], 0.5, rx[0:rows, :], ALU.mult, ALU.mult)
                    else:
                        tt(acc_taken, out, acc[j % 2][0:rows, :], rx[0:rows, :], ALU.mult)

                def rope(x, rows):
                    tt(None, temp[0:rows, :], x[0:rows], cos[0:rows], ALU.mult, go=True)
                    for b in range(0, rows, 64):
                        for s, o in ((b, b + 32), (b + 32, b)):
                            tt(None, temp2[o:o + 32, :], x[s:s + 32], sin[s:s + 32], ALU.mult,
                               go=(b, o) != (rows - 64, b))

                taps_open = [False]
                taps = [(j + i, k) for j in (0, 2) for k in range(CONV_K) for i in range(2)]

                def convolve(n):
                    for _ in range(min(n, len(taps))):
                        j, k = taps.pop(0)
                        src = glu[:, j, k:k + SEQ]
                        wt = par("dww", CONV_K * j + k)
                        if k == 0:
                            ins = nc.vector.tensor_scalar(cacc[:, j, :], src, wt, par("dwb", j), ALU.mult, ALU.add)
                        else:
                            dve.wait_ge(tap_done.sem, tap_done.at(layer, CONV_K * 4 - len(taps) - 2))
                            ins = nc.vector.scalar_tensor_tensor(out=cacc[:, j, :], in0=src, scalar=wt,
                                                                 in1=cacc[:, j, :], op0=ALU.mult, op1=ALU.add)
                        ins.then_inc(tap_done.sem, 1)

                dve.wait_ge(params_ready.sem, params_ready.at(layer, 1))
                ts(None, par("scw", 0, 10 * SSD_K + 10), par("scw", 0, 10 * SSD_K + 10), 0.5, ALU.mult)
                for u in range(RING - 1):
                    split(u)
                for k in range(KX):
                    if k == 6:
                        split(RING - 1)
                    dve.wait_ge(h_hi.sem, h_hi.at(layer, k + 1))
                    nc.vector.scalar_tensor_tensor(out=hlo[:, k, :], in0=xg[:, k, :], scalar=par("norm_g", k),
                                                           in1=hhi[:, k, :].bitcast(F32), op0=ALU.mult,
                                                           op1=ALU.subtract).then_inc(h_lo.sem, 1)

                def split_branch(first, end):
                    for k in range(first, end):
                        dve.wait_ge(h_hi.sem, h_hi.at(layer, KX + k + 1))
                        nc.vector.tensor_tensor(hlo[:, k, :], xg[:, k, :], hhi[:, k, :].bitcast(F32),
                                                ALU.subtract).then_inc(h_lo.sem, 1)

                def finish_xbc(i):
                    ch = XBC_CHANNELS[i]
                    o = xb[i // 5][:, i % 5, :]
                    dve.wait_ge(tap3_done.sem, tap3_done.at(layer, i + 1))
                    for k in range(3):
                        stt(tanh_in if k == 2 else None, o, raw[:, k:k + SEQ], par("scw", SSD_K * ch + k), o,
                            ALU.mult, ALU.add)
                    silu(xb_ready, o, o)

                for name, args, own in STEPS:
                    for u in own:
                        split(u + RING)
                    if name == "in" and args == (17, 0):
                        taps_open[0] = True
                    if name == "in" and args[1] == 0 and 34 <= 2 * args[0] < 54:
                        convolve(2)
                    if name == "in" and args[1] == 0 and 2 * args[0] >= 54:
                        convolve(2)
                    if name == "in" and args[1] == 1:
                        j = args[0]
                        kind, i, _ = TILES[j]
                        if kind in ("cq", "ckv"):
                            evac(j, temp[:, :])
                            sq = sqc if kind == "cq" else sqkv
                            if i == 0:
                                tt(lat_sq, sq, temp[:, :], temp[:, :], ALU.mult)
                            else:
                                tt(None, temp2[:, :], temp[:, :], temp[:, :], ALU.mult)
                                tt(lat_sq, sq, sq, temp2[:, :], ALU.add)
                            n = i + (0 if kind == "cq" else 4)
                            dve.wait_ge(cq_hi.sem, cq_hi.at(layer, n + 1))
                            hi, lo, g = (cqhi, cqlo, "qa") if kind == "cq" else (ckvhi, ckvlo, "kva")
                            stt(lat_lo, lo[:, i, :], temp[:, :], par(g, i), hi[:, i, :].bitcast(F32), ALU.mult,
                                ALU.subtract)
                        elif kind == "kpe":
                            d(None, nc.vector.memset(kd[64:128], 0.0))
                            evac(j, kd[0:76], rows=76)
                            mark(kd_ready)
                            tt(None, sqkp[0:64, :], kd[0:64], kd[0:64], ALU.mult)
                            ts(None, kr2[0:64, :], kd[0:64], par("kr")[0:64], ALU.mult)
                            rope(kr2[:, :], 64)
                            tt(kr_half, kr2[0:64, :], temp[0:64, :], temp2[0:64, :], ALU.add)
                        elif kind in ("gmla", "gconv"):
                            if kind == "gconv" and i == 0:
                                dve.wait_ge(scores_done.sem, scores_done.at(layer, 24))
                            evac(j, temp[:, :], half=True)
                            mark(tanh_in)
                            silu(None, xg[:, i if kind == "gmla" else 6 + i, :], temp[:, :])
                        elif kind == "z":
                            evac(j, temp[:, :], half=True)
                            mark(tanh_in)
                            silu(None, temp[:, :], temp[:, :])
                            tt(None, xg[:, 10 + i, :], xg[:, 10 + i, :], temp[:, :], ALU.mult)
                            if i == 5:
                                split_branch(0, 3)
                            if i == 0:
                                tt(None, sqz[:, :], xg[:, 10, :], xg[:, 10, :], ALU.mult)
                            else:
                                tt(None, temp[:, :], xg[:, 10 + i, :], xg[:, 10 + i, :], ALU.mult)
                                tt(ssd_sq if i == 5 else None, sqz[:, :], sqz[:, :], temp[:, :], ALU.add)
                        elif kind == "ua":
                            if i == 0:
                                dve.wait_ge(unit_used.sem, unit_used.at(layer, UNITS.index(("qrkn", 2)) + 1))
                            d(None, nc.vector.memset(glu[:, i, 0:PADC], 0.0))
                            evac(j, glu[:, i, PADC:PADC + SEQ], half=True)
                        elif kind == "ug":
                            evac(j, temp[:, :], half=True)
                            mark(tanh_in)
                            silu(None, glu[:, i, PADC:PADC + SEQ], glu[:, i, PADC:PADC + SEQ])
                        elif kind == "xbc":
                            if i == 0:
                                dve.wait_ge(scores_done.sem, scores_done.at(layer, 16))
                            d(None, nc.vector.memset(raw[:, 0:3], 0.0))
                            evac(j, raw[:, 3:3 + SEQ])
                            if not finished_in_attention(j):
                                convolve(1)
                                finish_xbc(i)
                    elif name == "kd_turn":
                        dve.wait_ge(kd_turned.sem, kd_turned.at(layer, 1))
                        v3 = lambda ap: ap.rearrange("p (c h) -> p c h", c=NT)
                        bias = par("dtb", 0, SSD_HEADS).unsqueeze(1).to_broadcast([P, NT, SSD_HEADS])
                        turned = T[0][:, :].rearrange("p (c f) -> p c f", c=NT)[:, :, ROPE:ROPE + SSD_HEADS]
                        tt(None, v3(sa), turned, bias, ALU.add)
                        stt(dt_asked, sbb, sa, -1.0, sa, ALU.mult, ALU.max)
                        dve.wait_ge(dt_exp.sem, dt_exp.at(layer, 1))
                        ts(None, scc, sbb, 2.0, ALU.add)
                        d(None, nc.vector.reciprocal(scc, scc))
                        tt(None, sbb, sbb, scc, ALU.mult)
                        tt(None, scc, sbb, sbb, ALU.mult)
                        ts(None, dt48, scc, 1.0 / 17, ALU.mult)
                        for n in (15, 13, 11, 9, 7, 5, 3):
                            stt(None, dt48, dt48, 1.0 / n, scc, ALU.add, ALU.mult)
                        stt(None, dt48, dt48, 1.0, sbb, ALU.add, ALU.mult)
                        ts(None, sa, sa, 0.0, ALU.max)
                        stt(None, dt48, dt48, 2.0, sa, ALU.mult, ALU.add)
                        rate = aneg.unsqueeze(1).to_broadcast([P, NT, SSD_HEADS])
                        stt(da_ready, v3(da48), v3(dt48), -1.0, rate, ALU.mult, ALU.mult)
                    elif name == "proj":
                        p = args[0]
                        for i in range(5):
                            if i == 4 or (p == 2 and i == 3):
                                dve.wait_ge(unit_used.sem, unit_used.at(layer, own[1] + 1))
                            else:
                                dve.wait_ge(proj_done.sem, proj_done.at(layer, 4 * p + i + 1))
                            proj_scale = rcq if i < 3 else rckv
                            tt(proj_taken, QK[p][i], (S + T + [M])[i][:, :], proj_scale[:, :], ALU.mult)
                        dve.wait_ge(sq_part.sem, sq_part.at(layer, p + 1))
                        tt(None, sqh[0:64, 0, :], sqh[0:64, 0, :], temp2[0:64, :], ALU.add)
                        tt(None, sqh[64:128, 1, :], sqh[64:128, 1, :], temp2[64:128, :], ALU.add)
                        tt(None, sqh[0:64, 2, :], sqh[0:64, 2, :], sqkp[0:64, :], ALU.add)
                        tt(sq_ready, sqh[0:64, 3, :], sqh[0:64, 3, :], sqkp[0:64, :], ALU.add)
                    elif name == "head_apply":
                        p, h = args
                        q = QK[p]
                        dve.wait_ge(head_r.sem, head_r.at(layer, 4 * p + 4))
                        dve.wait_ge(kr_both.sem, kr_both.at(layer, 1))
                        r = slice(64 * h, 64 * h + 64)
                        stt(None, q[h], q[h], par("qn"), sqh[:, h, :], ALU.mult, ALU.mult, go=True)
                        stt(None, q[2][r], q[2][r], par("qr")[r], sqh[r, h, :], ALU.mult, ALU.mult, go=True)
                        stt(None, q[3 + h], q[3 + h], par("kn"), sqh[:, 2 + h, :], ALU.mult, ALU.mult, go=True)
                        tt(None, q[5][r], kr2[r, :], sqh[r, 2 + h, :], ALU.mult)
                    elif name == "rotate":
                        q = QK[args[0]]
                        rope(q[2], P)
                        tt(qk_ready, q[2], temp[:, :], temp2[:, :], ALU.add)
                    elif name == "attend":
                        n = args[0]
                        if n < 24:
                            qb, width = n % 4, (n % 4 + 1) * P
                            dve.wait_ge(scores_done.sem, scores_done.at(layer, n + 1))
                            diag = S[n % 2][:, qb * P:(qb + 1) * P]
                            tt(None, diag, diag, mask, ALU.add)
                            d(None, nc.vector.tensor_reduce(rmax, S[n % 2][:, 0:width], AX_X, ALU.max))
                            ts(max_ready, negm, rmax, -SCALE, ALU.mult)
                        if 2 <= n:
                            m = n - 2
                            h, q = m // 4, slice((m % 4) * P, (m % 4 + 1) * P)
                            dve.wait_ge(o_done.sem, o_done.at(layer, m + 1))
                            tt(o_taken, xg[:, h, q], O[:, q], xg[:, h, q], ALU.mult)
                        if n < 24:
                            if n >= 6:
                                convolve(2)
                            dve.wait_ge(exp_done.sem, exp_done.at(layer, n + 1))
                            d(rinv_ready, nc.vector.reciprocal(rinv, rsum))
                        if n % 2 == 1 and finished_in_attention((n + 27) // 2):
                            finish_xbc(TILES[(n + 27) // 2][1])
                        elif n >= 6:
                            convolve(2)
                    elif name == "ssd_a":
                        s = args[0]
                        g, c = s // NT, s % NT
                        own_t = slice(12 * c + 6 * g, 12 * c + 6 * g + 6)
                        b = slice(c * P, c * P + P)
                        dve.wait_ge(acsb_loaded.sem, acsb_loaded.at(layer, 16 * (s + 1)))
                        dve.wait_ge(acs_ready.sem, acs_ready.at(layer, 1))
                        if s:
                            dve.wait_ge(ssd_y.sem, ssd_y.at(layer, s))
                        tt(dte_in, dte, acsb[:, :, P - 1], acst[:, own_t], ALU.subtract, go=True)
                        for h in range(GH):
                            one = acst[:, 12 * c + 6 * g + h:12 * c + 6 * g + h + 1]
                            ts(seg_in if h == GH - 1 else None, mt[:, h, :], acsb[:, h, :], one, ALU.subtract, 0.0,
                               ALU.min, go=True)
                        convolve(1)
                        dve.wait_ge(ssd_turned.sem, ssd_turned.at(layer, s + 1))
                        x3 = lambda ap: ap.rearrange("p (h q) -> p h q", h=GH)
                        d(None, nc.vector.tensor_copy(btok[:, :], T[0][:, 384:512]), go=True)
                        tt(None, cbm[:, :], T[1][:, 0:P], until, ALU.mult, go=True)
                        tt(None, x3(xdt[:, :]), x3(T[0][:, 0:GH * SSD_P]),
                           dt48[:, own_t].unsqueeze(2).to_broadcast([P, GH, SSD_P]), ALU.mult)
                        dve.wait_ge(dte_exp.sem, dte_exp.at(layer, s + 1))
                        tt(None, x3(xw[:, :]), x3(xdt[:, :]), dte.unsqueeze(2).to_broadcast([P, GH, SSD_P]), ALU.mult,
                           go=True)
                        dve.wait_ge(ecs_exp.sem, ecs_exp.at(layer, s + 1))
                        d(None, nc.vector.tensor_copy(cd, ecs[:, :, P - 1]))
                        tt(None, ecs[:, :, :], ecs[:, :, :], xb[g][:, 4, b].unsqueeze(1).to_broadcast([P, GH, P]),
                           ALU.mult, go=True)
                        dve.wait_ge(seg_exp.sem, seg_exp.at(layer, s + 1))
                        tt(ssd_in, mt[:, :, :], mt[:, :, :], cbm[:, :].unsqueeze(1).to_broadcast([P, GH, P]), ALU.mult,
                           go=True)
                    elif name == "ssd_b":
                        s = args[0]
                        g, c = s // NT, s % NT
                        b = slice(c * P, c * P + P)
                        dve.wait_ge(ssd_y.sem, ssd_y.at(layer, s + 1))
                        if c < NT - 1:
                            if c:
                                s3 = state[:, :].rearrange("p (h q) -> p h q", h=GH)
                                tt(None, s3, s3, cd.unsqueeze(2).to_broadcast([P, GH, SSD_P]), ALU.mult)
                                tt(None, state[:, :], state[:, :], S[1][:, 0:GH * SSD_P], ALU.add)
                            else:
                                d(None, nc.vector.tensor_copy(state[:, :], S[1][:, 0:GH * SSD_P]))
                        for i in range(3):
                            stt(ssd_taken if i == 2 else None, xg[:, 10 + 3 * g + i, b], xb[g][:, i, b],
                                par("skip", 3 * g + i), S[0][:, i * P:(i + 1) * P], ALU.mult, ALU.add, go=i < 2)
                    elif name == "ln_mean":
                        convolve(len(taps))
                        dve.wait_ge(tap_done.sem, tap_done.at(layer, 4 * CONV_K))
                        tt(None, csum[:, :], cacc[:, 0, :], cacc[:, 1, :], ALU.add)
                        tt(None, csum[:, :], csum[:, :], cacc[:, 2, :], ALU.add)
                        tt(conv_sum_in, csum[:, :], csum[:, :], cacc[:, 3, :], ALU.add)
                        dve.wait_ge(conv_sum.sem, conv_sum.at(layer, 1))
                        for i in range(4):
                            stt(None, cacc[:, i, :], M[:, :], -1.0 / CONV_WIDTH, cacc[:, i, :], ALU.mult, ALU.add)
                        tt(None, csum[:, :], cacc[:, 0, :], cacc[:, 0, :], ALU.mult)
                        for i in range(1, 4):
                            tt(None, temp[:, :], cacc[:, i, :], cacc[:, i, :], ALU.mult)
                            tt(conv_sum_in if i == 3 else None, csum[:, :], csum[:, :], temp[:, :], ALU.add)
                    elif name == "ln_var":
                        dve.wait_ge(conv_r.sem, conv_r.at(layer, 1))
                        ts(None, par("lng", 0, 8), par("lng", 0, 8), 0.5, ALU.mult)
                        for i in range(4):
                            tt(None, temp[:, :], cacc[:, i, :], rckv[:, :], ALU.mult)
                            ts(None, temp[:, :], temp[:, :], par("lng", i), ALU.mult, par("lnb", i), ALU.add)
                            mark(tanh_in)
                            silu(pw_in, cacc[:, i, :], temp[:, :])
                            dve.wait_ge(pw_hi.sem, pw_hi.at(layer, i + 1))
                            tt(pw_lo, pwlo[:, i, :], cacc[:, i, :], pwhi[:, i, :].bitcast(F32), ALU.subtract)
                    elif name == "pw":
                        f = args[0]
                        dve.wait_ge(unit_used.sem, unit_used.at(layer, own[0] + 1))
                        tt(pw_taken, xg[:, 6 + f, :], [O, M][f % 2][:, :], xg[:, 6 + f, :], ALU.mult)
                    elif name == "ssd_sum":
                        split_branch(3, 10)
                        dve.wait_ge(ssd_r.sem, ssd_r.at(layer, 1))
                        for k in range(10, KX):
                            stt(branch_ready, xg[:, k, :], xg[:, k, :], par("sng", k - 10), rcq[:, :], ALU.mult,
                                ALU.mult, go=k < KX - 1)
                            if k >= 12:
                                split_branch(k - 2, k - 1)
                        split_branch(KX - 2, KX)
                    elif name == "out" and args[1] == 1:
                        f = args[0]
                        n = len(TILES) + f + 1
                        dve.wait_ge(unit_used.sem, unit_used.at(layer, TILE_UNIT[n - 1] + 1))
                        dve.wait_ge(res_loaded[f % 2].sem, res_loaded[f % 2].at(layer, 16 * (f // 2 + 1)))
                        if f == 0:
                            dve.wait_ge(h_lo.sem, h_lo.at(layer, 2 * KX))
                        tt(acc_taken, xg[:, f, :], acc[(f + 1) % 2][:, :], xr[f % 2][:, :], ALU.add)
                        mark(x_ready)
                        if f == 0:
                            tt(None, sqx, xg[:, 0, :], xg[:, 0, :], ALU.mult)
                        else:
                            tt(None, temp[:, :], xg[:, f, :], xg[:, f, :], ALU.mult)
                            tt(sqx_ready if f == KX - 1 else None, sqx, sqx, temp[:, :], ALU.add)

        assert (act_chain.made, dve_chain.made) == (ACT_CHAIN, DVE_CHAIN), (act_chain.made, dve_chain.made)


def host_weights(w_in, w_q_b, w_kv_b, conv_pw_w, w_out):
    q_heads = w_q_b.reshape(DEPTH, 4, P, HEADS, QK_HEAD)
    kv_heads = w_kv_b.reshape(DEPTH, 2, P, HEADS, NOPE + VDIM)
    w_in = w_in.reshape(DEPTH, KX, P, -1)
    pw = conv_pw_w.reshape(DEPTH, 4, P, CONV_WIDTH)
    w_out = w_out.reshape(DEPTH, KX, P, D_MODEL)

    def rows(blocks):
        return blocks.transpose(0, 2, 1, 3).reshape(DEPTH, P, -1)

    out = []
    for kind, *args in UNITS:
        if kind == "in":
            j, half = args
            blocks = np.concatenate([w_in[:, 8 * half:8 * half + 8, :, c:c + n] for c, n in TILES[j][2]], axis=3)
            block = rows(blocks)
        elif kind == "v":
            h = 3 * args[0]
            block = rows(kv_heads[:, :, :, h:h + 3, NOPE:].reshape(DEPTH, 2, P, 3 * VDIM))
        elif kind == "qn":
            h = 2 * args[0]
            block = np.concatenate([rows(q_heads[:, :, :, h + i, :NOPE]) for i in range(2)], axis=2)
        elif kind == "qrkn":
            h = 2 * args[0]
            rope = rows(q_heads[:, :, :, h:h + 2, NOPE:].reshape(DEPTH, 4, P, 2 * ROPE))
            block = np.concatenate([rope] + [rows(kv_heads[:, :, :, h + i, :NOPE]) for i in range(2)], axis=2)
        elif kind == "pw":
            block = rows(pw[:, :, :, P * args[0]:P * args[0] + P])
        else:
            f, half = args
            block = rows(w_out[:, 8 * half:8 * half + 8, :, P * f:P * f + P])
        out.append(block.reshape(DEPTH, -1))
    return np.concatenate(out, axis=1)


def host_params(a):
    def feature(v):
        return v.reshape(DEPTH, -1, P).transpose(0, 2, 1)

    def taps(v):
        return v.reshape(DEPTH, v.shape[1], -1, P).transpose(0, 3, 2, 1).reshape(DEPTH, P, -1)

    def twice(v):
        return np.concatenate([v, v], axis=1)[:, :, None]

    def every(v):
        return np.broadcast_to(v[:, None, :], (DEPTH, P, v.shape[1]))

    qn, kn = a["q_norm"], a["k_norm"]
    parts = {
        "norm_g": feature(a["norm_g"]), "qa": feature(a["q_a_norm"]), "kva": feature(a["kv_a_norm"]),
        "qn": qn[:, :NOPE, None], "qr": twice(qn[:, NOPE:]), "kn": kn[:, :NOPE, None], "kr": twice(kn[:, NOPE:]),
        "dww": taps(a["conv_dw_w"]), "dwb": feature(a["conv_dw_b"]), "lng": feature(a["conv_ln_g"]),
        "lnb": feature(a["conv_ln_b"]), "scw": taps(a["ssd_conv_w"]), "scb": feature(a["ssd_conv_b"]),
        "skip": feature(np.repeat(a["ssd_D"], SSD_P, axis=1)), "sng": feature(a["ssd_norm_g"]),
        "dtb": every(a["ssd_dt_bias"]), "alog": every(a["ssd_A_log"]),
    }
    table = np.concatenate([parts[n] for n in PARAM_COLS], axis=2)
    return np.concatenate([table, np.zeros_like(table[:1])], axis=0).reshape((DEPTH + 1) * P, NPAR)


def host_consts():
    half = ROPE // 2
    freq = np.float32(ROPE_THETA) ** (-np.arange(half, dtype=np.float32) / np.float32(half))
    angle = np.arange(SEQ, dtype=np.float32)[:, None] * freq[None, :].astype(np.float32)
    c, s = np.cos(angle).T.astype(np.float32), np.sin(angle).T.astype(np.float32)
    i = np.arange(P)
    return np.concatenate([
        np.concatenate([c, c, c, c]), np.concatenate([s, -s, s, -s]), np.eye(P),
        (i[:, None] <= i[None, :]), np.where(i[None, :] <= i[:, None], 0.0, -1e30)], axis=1).astype(np.float32)


def kernel(x, **a):
    import concourse.bacc as bacc
    from concourse.bass_utils import run_bass_kernel_spmd

    a = {n: np.asarray(v) for n, v in a.items()}
    feature_x = np.asarray(x)[0].T.reshape(KX, P, SEQ).transpose(1, 0, 2).reshape(P, KX * SEQ)
    arrays = {
        "x_features": np.ascontiguousarray(feature_x),
        "weights": host_weights(a["w_in"], a["w_q_b"], a["w_kv_b"], a["conv_pw_w"], a["w_out"]),
        "params": host_params(a),
        "consts": host_consts(),
    }
    nc = bacc.Bacc("TRN2", target_bir_lowering=False, num_devices=1)
    args = [nc.dram_tensor(n, v.shape, F32, kind="ExternalInput").ap() for n, v in arrays.items()]
    args.append(nc.dram_tensor("y_features", (P, KX * SEQ), F32, kind="ExternalOutput").ap())
    args.append(nc.dram_tensor("acs_rows", (NT * SSD_HEADS, P), F32).ap())
    hybrid_kernel(nc, *args)
    got = run_bass_kernel_spmd(nc, [arrays], core_ids=[0]).results[0]["y_features"]
    return got.reshape(P, KX, SEQ).transpose(2, 1, 0).reshape(1, SEQ, D_MODEL)
```
